# Optimizing a Trainium2 kernel written in Bass

```python
import math
import jax, jax.numpy as jnp
from jax import lax
import numpy as np

D_MODEL = 1024
BATCH = 1
SEQ = 1024
DEPTH = 1

EPS = 1e-6
D_CONV = D_MODEL // 2
CONV_K = 3
HEAD_DIM = 64
N_HEADS = (D_MODEL // 2) // HEAD_DIM
N_KV_HEADS = 2
GQA_GROUP = N_HEADS // N_KV_HEADS
D_ATTN = N_HEADS * HEAD_DIM
D_KV = N_KV_HEADS * HEAD_DIM
WINDOW = 128
BLK = 128
D_MIX = D_CONV + D_ATTN
D_IN_PROJ = 3 * D_CONV + D_ATTN + 2 * D_KV
N_EXPERTS = 64
TOP_K = 8
N_GROUPS = 8
TOPK_GROUPS = 4
D_EXPERT = D_MODEL // 4
ROUTED_SCALE = 2.5
MOE_BLK = 128

kernel_name = "hymba_conv_swa_sink_alibi_moe_block"

def _alibi_slopes(n_heads):
    return np.array([2.0 ** (-8.0 * (h + 1) / n_heads) for h in range(n_heads)], dtype=np.float32)

def rms_norm(x, w):
    xf = x.astype(jnp.float32)
    y = xf * lax.rsqrt(jnp.mean(xf * xf, axis=-1, keepdims=True) + EPS)
    return (y * w.astype(jnp.float32)).astype(x.dtype)

def short_conv_mixer(b_gate, c_gate, h, conv_w):
    S = h.shape[1]
    u = c_gate * h
    u_pad = jnp.pad(u, ((0, 0), (CONV_K - 1, 0), (0, 0)))
    v = conv_w[0] * u_pad[:, 0:S]
    for k in range(1, CONV_K):
        v = v + conv_w[k] * u_pad[:, k:k + S]
    return b_gate * v

def sliding_window_attention(q, k, v, sinks):
    Bsz, S = q.shape[0], q.shape[1]
    nb = S // BLK
    qb = q.reshape(Bsz, nb, BLK, N_KV_HEADS, GQA_GROUP, HEAD_DIM)
    kb = k.reshape(Bsz, nb, BLK, N_KV_HEADS, HEAD_DIM)
    vb = v.reshape(Bsz, nb, BLK, N_KV_HEADS, HEAD_DIM)
    pad = ((0, 0), (1, 0), (0, 0), (0, 0), (0, 0))
    kk = jnp.concatenate([jnp.pad(kb, pad)[:, :-1], kb], axis=2)
    vv = jnp.concatenate([jnp.pad(vb, pad)[:, :-1], vb], axis=2)
    s = jnp.einsum('bnqhgd,bnkhd->bhgnqk', qb, kk,
                   preferred_element_type=jnp.float32) * (HEAD_DIM ** -0.5)
    qi = jnp.arange(BLK)[:, None]
    kj = jnp.arange(2 * BLK)[None, :]
    dist = qi - kj + BLK
    key_pos = jnp.arange(nb)[:, None, None] * BLK - BLK + kj[None]
    mask = (dist >= 0)[None] & (dist < WINDOW)[None] & (key_pos >= 0)
    slopes = jnp.asarray(_alibi_slopes(N_HEADS)).reshape(N_KV_HEADS, GQA_GROUP)
    bias = -slopes[:, :, None, None, None] * dist.astype(jnp.float32)[None, None, None]
    s = jnp.where(mask, s + bias, -jnp.inf)
    sink = jnp.broadcast_to(
        sinks.astype(jnp.float32).reshape(1, N_KV_HEADS, GQA_GROUP, 1, 1, 1),
        s.shape[:-1] + (1,))
    p = jax.nn.softmax(jnp.concatenate([s, sink], axis=-1), axis=-1)[..., :-1]
    o = jnp.einsum('bhgnqk,bnkhd->bnqhgd', p.astype(vv.dtype), vv)
    return o.reshape(Bsz, S, N_HEADS * HEAD_DIM)

def swiglu(x, w_gate, w_up, w_down):
    return (jax.nn.silu(x @ w_gate) * (x @ w_up)) @ w_down

def moe_ffn(xf, w_router, router_bias, w_eg, w_eu, w_ed, w_sg, w_su, w_sd):
    N, D = xf.shape
    scores = jax.nn.sigmoid(xf.astype(jnp.float32) @ w_router.astype(jnp.float32))
    biased = scores + router_bias.astype(jnp.float32)
    grp = biased.reshape(N, N_GROUPS, N_EXPERTS // N_GROUPS)
    grp_score = lax.top_k(grp, 2)[0].sum(-1)
    _, top_groups = lax.top_k(grp_score, TOPK_GROUPS)
    group_mask = jax.nn.one_hot(top_groups, N_GROUPS, dtype=jnp.float32).sum(1) > 0
    expert_mask = jnp.repeat(group_mask, N_EXPERTS // N_GROUPS, axis=1)
    _, top_idx = lax.top_k(jnp.where(expert_mask, biased, -jnp.inf), TOP_K)
    top_w = jnp.take_along_axis(scores, top_idx, axis=1)
    top_w = top_w / jnp.sum(top_w, axis=-1, keepdims=True) * ROUTED_SCALE

    A = N * TOP_K
    flat_e = top_idx.reshape(-1)
    flat_tok = jnp.repeat(jnp.arange(N, dtype=jnp.int32), TOP_K)
    flat_w = top_w.reshape(-1)
    order = jnp.argsort(flat_e)
    sorted_e = flat_e[order]
    counts = jnp.bincount(flat_e, length=N_EXPERTS)
    starts = jnp.cumsum(counts) - counts
    padded = (counts + MOE_BLK - 1) // MOE_BLK * MOE_BLK
    pad_end = jnp.cumsum(padded)
    pad_start = pad_end - padded
    dest = pad_start[sorted_e] + (jnp.arange(A) - starts[sorted_e])
    n_blocks = -(-A // MOE_BLK) + N_EXPERTS
    P = n_blocks * MOE_BLK
    buf_tok = jnp.full((P,), N, dtype=jnp.int32).at[dest].set(flat_tok[order])
    buf_w = jnp.zeros((P,), jnp.float32).at[dest].set(flat_w[order])
    block_e = jnp.clip(jnp.searchsorted(pad_end, jnp.arange(n_blocks) * MOE_BLK, side='right'),
                       0, N_EXPERTS - 1)
    x_pad = jnp.concatenate([xf, jnp.zeros((1, D), xf.dtype)], axis=0)

    def expert_block(args):
        tok, e = args
        xb = x_pad[tok]
        return swiglu(xb, w_eg[e], w_eu[e], w_ed[e])

    y = lax.map(expert_block, (buf_tok.reshape(n_blocks, MOE_BLK), block_e)).reshape(P, D)
    y = y * buf_w[:, None].astype(y.dtype)
    routed = jnp.zeros((N + 1, D), y.dtype).at[buf_tok].add(y)[:N]
    return routed + swiglu(xf, w_sg, w_su, w_sd)

def setup_inputs(seed: int = 0) -> dict:
    key = jax.random.key(seed)
    ks = jax.random.split(key, 20)
    f32 = jnp.float32
    nrm = lambda k, shape, scale: jax.random.normal(k, shape, f32) * scale
    gain = lambda k, shape: 1.0 + 0.02 * jax.random.normal(k, shape, f32)
    L = DEPTH
    return {
        "x": jax.random.normal(ks[0], (BATCH, SEQ, D_MODEL), f32),
        "mix_norm_w": gain(ks[1], (L, D_MODEL)),
        "w_in": nrm(ks[2], (L, D_MODEL, D_IN_PROJ), D_MODEL ** -0.5),
        "conv_w": nrm(ks[3], (L, CONV_K, D_CONV), CONV_K ** -0.5),
        "q_norm_w": gain(ks[4], (L, HEAD_DIM)),
        "k_norm_w": gain(ks[5], (L, HEAD_DIM)),
        "sinks": nrm(ks[6], (L, N_HEADS), 0.5),
        "conv_out_norm_w": gain(ks[7], (L, D_CONV)),
        "attn_out_norm_w": gain(ks[8], (L, D_ATTN)),
        "w_out": nrm(ks[9], (L, D_MIX, D_MODEL), D_MIX ** -0.5),
        "ffn_norm_w": gain(ks[10], (L, D_MODEL)),
        "w_router": nrm(ks[11], (L, D_MODEL, N_EXPERTS), D_MODEL ** -0.5),
        "router_bias": nrm(ks[12], (L, N_EXPERTS), 0.01),
        "w_exp_gate": nrm(ks[13], (L, N_EXPERTS, D_MODEL, D_EXPERT), D_MODEL ** -0.5),
        "w_exp_up": nrm(ks[14], (L, N_EXPERTS, D_MODEL, D_EXPERT), D_MODEL ** -0.5),
        "w_exp_down": nrm(ks[15], (L, N_EXPERTS, D_EXPERT, D_MODEL), D_EXPERT ** -0.5),
        "w_sh_gate": nrm(ks[16], (L, D_MODEL, D_EXPERT), D_MODEL ** -0.5),
        "w_sh_up": nrm(ks[17], (L, D_MODEL, D_EXPERT), D_MODEL ** -0.5),
        "w_sh_down": nrm(ks[18], (L, D_EXPERT, D_MODEL), D_EXPERT ** -0.5),
    }

def reference(x, mix_norm_w, w_in, conv_w, q_norm_w, k_norm_w, sinks, conv_out_norm_w,
              attn_out_norm_w, w_out, ffn_norm_w, w_router, router_bias, w_exp_gate,
              w_exp_up, w_exp_down, w_sh_gate, w_sh_up, w_sh_down):
    Bsz, S, D = x.shape
    for l in range(DEPTH):
        u = rms_norm(x, mix_norm_w[l])
        proj = u @ w_in[l]
        b_gate, c_gate, h, q, k, v = jnp.split(
            proj, np.cumsum([D_CONV, D_CONV, D_CONV, D_ATTN, D_KV]).tolist(), axis=-1)
        y_conv = short_conv_mixer(b_gate, c_gate, h, conv_w[l])
        q = rms_norm(q.reshape(Bsz, S, N_HEADS, HEAD_DIM), q_norm_w[l])
        k = rms_norm(k.reshape(Bsz, S, N_KV_HEADS, HEAD_DIM), k_norm_w[l])
        v = v.reshape(Bsz, S, N_KV_HEADS, HEAD_DIM)
        y_attn = sliding_window_attention(q, k, v, sinks[l])
        y_mix = jnp.concatenate([rms_norm(y_conv, conv_out_norm_w[l]),
                                 rms_norm(y_attn, attn_out_norm_w[l])], axis=-1)
        x = x + y_mix @ w_out[l]
        xn = rms_norm(x, ffn_norm_w[l]).reshape(Bsz * S, D)
        x = x + moe_ffn(xn, w_router[l], router_bias[l], w_exp_gate[l], w_exp_up[l],
                        w_exp_down[l], w_sh_gate[l], w_sh_up[l], w_sh_down[l]).reshape(Bsz, S, D)
    return x


_drawn_inputs = setup_inputs


def setup_inputs(seed=0):
    import zlib

    import numpy as np

    out = dict(_drawn_inputs(seed))
    spreads = {}
    factors = {}
    for name, (base, spread) in spreads.items():
        noise = np.random.default_rng([zlib.crc32(name.encode()), seed]).standard_normal(out[name].shape)
        drawn = base * np.exp(spread * noise) if base else spread * noise
        out[name] = __import__('jax').numpy.asarray(drawn.astype(out[name].dtype))
    for name, factor in factors.items():
        out[name] = (out[name] * factor).astype(out[name].dtype)
    return out
```

```python
from contextlib import ExitStack

import concourse.bass as bass
from concourse import mybir

F32 = mybir.dt.float32
BF16 = mybir.dt.bfloat16
I32 = mybir.dt.int32
ALU = mybir.AluOpType
ACT = mybir.ActivationFunctionType
AX = mybir.AxisListType

P = 128
EPS = 1e-6
BIG = 1e30
SCALE_ROUTED = 2.5


class Tile:

    def __init__(self, t, par, half):
        self.t, self.par, self.half = t, par, half

    def next(self):
        return Tile(self.t + 1, 1 - self.par, self.half + self.par)

    def prev(self):
        return Tile(self.t - 1, 1 - self.par, self.half - (1 - self.par))


def hymba_moe(nc, x, mix_norm_w, w_in, conv_w, q_norm_w, k_norm_w, sinks, conv_out_norm_w, attn_out_norm_w,
              w_out, ffn_norm_w, w_router, router_bias, w_exp_gate, w_exp_up, w_exp_down, w_sh_gate, w_sh_up,
              w_sh_down, out):
    S, D = x.shape[1], x.shape[2]
    DC = conv_w.shape[2]
    HD = q_norm_w.shape[1]
    NH = sinks.shape[1]
    DA = NH * HD
    DIN = w_in.shape[2]
    DKV = (DIN - 3 * DC - DA) // 2
    NKV = DKV // HD
    HP = NH // NKV
    NE = w_router.shape[2]
    FE = w_exp_gate.shape[3]
    NG, TOPG, TOPK = 8, 4, 8
    EG = NE // NG
    NT = S // P
    KT = D // P
    FT = FE // P
    assert NT == 8 and KT == 8 and NKV == 2 and DC == DA == 512 and FT == 2
    JMAX = S * TOPK // P + NE
    JT = JMAX + 6
    MIN_JOBS = S * TOPK // P
    NSLOT = 4
    NSH = NT
    SLOTW = 3 * KT * FE

    x2, out2 = x[0], out[0]

    with ExitStack() as ctx:
        def sb(name, shape, dt=F32):
            return ctx.enter_context(nc.sbuf_tensor(name, shape, dt))

        def sem(name):
            return ctx.enter_context(nc.semaphore(name))

        u_dram = nc.dram_tensor("u_dram", [S + 2, DC], F32).ap()
        xn_dram = nc.dram_tensor("xn_dram", [S, D], F32).ap()
        x1_dram = nc.dram_tensor("x1_dram", [S, D], F32).ap()
        table = nc.dram_tensor("job_table", [P * JT, 2], F32).ap()

        psP = ctx.enter_context(nc.psum_tensor("psP", [P, 2, 512], F32))
        psT = ctx.enter_context(nc.psum_tensor("psT", [P, 8, 128], F32))
        psW = ctx.enter_context(nc.psum_tensor("psW", [P, 4, 512], F32))

        WIN = KT * DIN
        wts = sb("wts", [P, WIN + KT * D])
        w_in_sb = wts[:, 0:WIN].rearrange("p (k n) -> p k n", k=KT)
        w_out_sb = wts[:, WIN:WIN + KT * D].rearrange("p (k n) -> p k n", k=KT)
        assert WIN == 3 * SLOTW and KT * D >= SLOTW

        ident = sb("ident", [P, P])
        minus_half = sb("minus_half", [P, 16])
        ones_bf = sb("ones_bf", [P, P], BF16)
        tri_bf = sb("tri_bf", [P, P], BF16)
        upper_bf = sb("upper_bf", [NE, 2 * NE], BF16)
        gtri = sb("gtri", [P, NG, NG])
        bias = sb("bias", [P, NH, 2 * P])
        iota_j = sb("iota_j", [NE, JT])
        mixw = sb("mixw", [P, KT])
        outw = sb("outw", [P, KT])
        qw = sb("qw", [P, 1])
        kw = sb("kw", [P, 1])
        sink = sb("sink", [P, NH])
        convw = sb("convw", [P, 3, DC])
        ffnw = sb("ffnw", [P, D])
        rbias = sb("rbias", [P, NE])
        wr = sb("wr", [P, KT, NE])
        zrow = sb("zrow", [2, DC])
        one_col = sb("one_col", [P, 1])

        AREA = 14 * 1024
        area = sb("area", [P, AREA])
        at = [0]

        def cut(words):
            at[0] += words
            assert at[0] <= AREA
            return area[:, at[0] - words:at[0]]

        x_sb = cut(2 * D).rearrange("p (b n) -> p b n", b=2)
        s_sb = cut(NH * 2 * P).rearrange("p (h k) -> p h k", h=NH)
        pT = cut(NH * 2 * P).rearrange("p (h k) -> p h k", k=P)
        xs = xn = cut(D)
        uT = cut(D).rearrange("p (k n) -> p k n", k=KT)
        yT = xnT = cut(D).rearrange("p (k n) -> p k n", k=KT)
        ys = x1 = cut(D)
        y_conv = cut(DC)
        y_attn = cut(DA)
        c_sb, h_sb, b_sb, q_sb = cut(DC), cut(DC), cut(DC), cut(DA)
        u1, u2 = cut(DC), cut(DC)
        setup = pT.rearrange("p h k -> p (h k)")
        dist_i = setup[:, 0:2 * P].bitcast(I32)
        dist = setup[:, 2 * P:4 * P]
        far = setup[:, 4 * P:6 * P]
        far_b = setup[:, 6 * P:8 * P]
        iota_ji = setup[0:NE, 8 * P:8 * P + JT].bitcast(I32)
        job0 = setup[:, 10 * P:10 * P + 2 * JT].rearrange("p (j c) -> p j c", c=2)
        job_i = setup[:, 13 * P:13 * P + JT].bitcast(I32).rearrange("p (j a) -> p j a", a=1)
        kv_sb = sb("kv_sb", [P, 2, 2 * DKV])
        u_sb = c_sb
        kn = sb("kn", [P, DKV])
        qT = sb("qT", [P, HP, P])
        kT = sb("kT", [P, 2, P])
        junk = sb("junk", [P, D], BF16)
        dsq = qn = sb("dsq", [P, DA])
        st_x = sb("st_x", [P, 3])
        st_q = sb("st_q", [P, 3, NH + NKV])
        st_s = sb("st_s", [P, 8, NH])
        st_y = sb("st_y", [P, 3, 2])
        st_n = sb("st_n", [P, 3])
        sc = sb("sc", [P, NE])
        bi = sb("bi", [P, NE])
        mb = sb("mb", [P, NE])
        mr = sb("mr", [P, NE])
        g8 = sb("g8", [P, NG, 8])
        gs = sb("gs", [P, NG])
        gcmp = sb("gcmp", [P, NG, NG])
        geq = sb("geq", [P, NG, NG])
        rank = sb("rank", [P, NG])
        top = sb("top", [P, 8])
        wsum = sb("wsum", [P, 2])
        w_all = sb("w_all", [P, NT, NE])
        m_all = sb("m_all", [P, NT, NE], BF16)
        msum = sb("msum", [P, NT + 1, NE], BF16)
        pos = sb("pos", [P, NT, NE])

        at[0] = 0
        xg = cut(2 * D).rearrange("p (b n) -> p b n", b=2)
        ysb = cut(2 * D).rearrange("p (b n) -> p b n", b=2)
        x1l = cut(2 * D).rearrange("p (b n) -> p b n", b=2)
        xT = cut(D).rearrange("p (k n) -> p k n", k=KT)
        sg = cut(FE)
        hh = cut(FE)
        hT = cut(FE).rearrange("p (f n) -> p f n", f=FT)
        posi = cut(NT * NE).bitcast(I32)
        chunk = cut(NT * NE)
        within = cut(NT * NE)
        addr = cut(NT * NE).rearrange("p (t e) -> p t e", t=NT)
        eq = cut(8 * NE).rearrange("p (j e) -> p j e", j=8)
        base = cut(2 * NE)
        nbf = cut(NE)
        tab = cut(2 * JT).rearrange("p (j c) -> p j c", c=2)
        cnt_i = sb("cnt_i", [NE, 2], I32)
        nb_bf = sb("nb_bf", [NE, 1], BF16)
        nb_row = sb("nb_row", [NE, P], BF16)
        jend_col = sb("jend_col", [NE, 1])
        ended = sb("ended", [NE, JT], BF16)
        ring_i = sb("ring_i", [P, JT + 1], I32)
        jend_i = sb("jend_i", [P, NE], I32)
        n_jobs = sb("n_jobs", [P, 10], I32)
        tops = sb("tops", [P, NT, 8])
        slot_i = sb("slot_i", [P, NT * 8], I32)
        pay = sb("pay", [P, NT, 8, 2])
        tok_i = sb("tok_i", [P, NT, 8], I32)
        gidx = sb("gidx", [P, 2], I32)
        sidx = sb("sidx", [P, 2], I32)

        s_const_ld = sem("const_ld")
        s_mixw_ld = sem("mixw_ld")
        s_const_pool = sem("const_pool")
        s_const_dve = sem("const_dve")
        s_wout_ld = sem("wout_ld")
        s_init_st = sem("init_st")
        s_u_st = sem("u_st")
        s_u_ld = sem("u_ld")
        s_xn_st = sem("xn_st")
        s_x1_st = sem("x1_st")
        s_x_rms = sem("x_rms")
        s_x_scaled = sem("x_scaled")
        s_uT_ready = sem("uT_ready")
        s_tx = sem("tx")
        s_txn = sem("txn")
        s_tqk = sem("tqk")
        s_ty = sem("ty")
        s_scores = sem("scores")
        s_pt = sem("pt")
        s_pv = sem("pv")
        s_proj = sem("proj")
        s_proj_out = sem("proj_out")
        s_logits = sem("logits")
        s_position = sem("position")
        s_outproj = sem("outproj")
        s_qk_norm = sem("qk_norm")
        s_qkT = sem("qkT")
        s_soft = sem("soft")
        s_exps = sem("exps")
        s_pT_ready = sem("pT_ready")
        s_o_norm = sem("o_norm")
        s_y_sq = sem("y_sq")
        s_y_rms = sem("y_rms")
        s_y_scaled = sem("y_scaled")
        s_yT_ready = sem("yT_ready")
        s_u_ready = sem("u_ready")
        s_conv = sem("conv")
        s_x1_ready = sem("x1_ready")
        s_x1_sq = sem("x1_sq")
        s_xn_ready = sem("xn_ready")
        s_xnT_ready = sem("xnT_ready")
        s_sigm = sem("sigm")
        s_route = sem("route")
        s_pos_ready = sem("pos_ready")
        s_pre_pe = sem("pre_pe")
        s_post = sem("post")
        s_post_pe = sem("post_pe")
        s_n_jobs = sem("n_jobs_ready")
        s_post_idx = sem("post_idx")
        s_sc_tab = sem("sc_tab")
        s_xg_t = sem("xg_t")
        s_gu = sem("gu")
        s_silu = sem("silu")
        s_h_ready = sem("h_ready")
        s_th = sem("th")
        s_hT_ready = sem("hT_ready")
        s_down = sem("down")
        s_y_ready = sem("y_ready")
        s_xT_ready = sem("xT_ready")
        s_idx_cp = sem("idx_cp")
        s_added = sem("added")
        s_x_sq = sem("x_sq")
        x_ld = [sem(f"x_ld{b}") for b in range(2)]
        g_ld = [sem(f"g_ld{b}") for b in range(2)]
        r_ld = [sem(f"r_ld{b}") for b in range(2)]
        sh_st = [sem(f"sh_st{b}") for b in range(2)]
        sh_x1 = [sem(f"sh_x1{b}") for b in range(2)]
        win_ld = [sem(f"win_ld_{g}") for g in ("c", "h", "b", "q", "kv")]
        w_ld = [sem(f"w_ld{b}") for b in range(NSLOT)]

        carried = {e.engine: sem(f"carried_{n}") for n, e in
                   (("sp", nc.sync), ("pool", nc.gpsimd), ("dve", nc.vector))}
        N_CONST = 11
        GROUPS = [("c", DC, DC), ("h", 2 * DC, DC), ("b", 0, DC), ("q", 3 * DC, DA), ("kv", 3 * DC + DA, 2 * DKV)]
        NGR = len(GROUPS)
        N_RT = NG + 17

        def front(eng, step):
            step(Tile(0, 0, 0), True, False)
            with eng.Fori(0, (NT - 2) // 2) as i:
                step(Tile(2 * i + 1, 1, i), False, False)
                step(Tile(2 * i + 2, 0, i + 1), False, False)
            step(Tile(NT - 1, 1, NT // 2 - 1), False, True)

        def routed_jobs(eng, c, jobs):
            pairs = eng.value_load(n_jobs[0:1, 2 + c:3 + c], min_val=MIN_JOBS // 2 - c, max_val=JMAX // 2)
            full = eng.value_load(n_jobs[0:1, 4 + c:5 + c], min_val=MIN_JOBS // 4 - c, max_val=JMAX // 4)
            with eng.Fori(0, full) as i:
                jobs(i * 2, (0, 1))
                jobs(i * 2 + 1, (0, 1))
            two = eng.alloc_register(f"two_{c}")
            eng.reg_load(two, n_jobs[0:1, 6 + c:7 + c])
            with eng.If_ne(two, 0):
                jobs(full * 2, (0, 1))
            one = eng.alloc_register(f"one_{c}")
            eng.reg_load(one, n_jobs[0:1, 8 + c:9 + c])
            with eng.If_ne(one, 0):
                jobs(pairs, (0,))
            return one

        def carry(eng):
            eng.sem_inc(carried[eng.engine], 1)

        def bc(ap, shape):
            return ap.to_broadcast(shape)

        block = ctx.enter_context(nc.Block())

        @block.sync
        def _(sp):
            def load_x(T):
                sp.dma_start(x_sb[:, T.par], x2[bass.ds(T.t * P, P), :]).then_inc(x_ld[T.par], 16)

            load_x(Tile(0, 0, 0))
            for g, (_, c0, n) in enumerate(GROUPS):
                sp.dma_start(w_in_sb[:, :, c0:c0 + n], w_in[0].rearrange("(k p) n -> p k n", p=P)[:, :, c0:c0 + n]) \
                  .then_inc(win_ld[g], 16)
                if g == 2:
                    sp.wait_ge(s_const_pool, 15)
            load_x(Tile(1, 1, 0))
            sp.dma_start(w_out_sb, w_out[0].rearrange("(k p) n -> p k n", p=P)).then_inc(s_wout_ld, 16)
            sp.wait_ge(s_const_dve, 6)
            sp.dma_start(table.rearrange("(p j) c -> p j c", p=P), job0[:, :, :]).then_inc(s_init_st, 16)
            sp.dma_start(u_dram[0:2, :], zrow[:, :]).then_inc(s_init_st, 16)
            sp.wait_ge(s_init_st, 32)

            def shift_u(T):
                sp.wait_ge(s_u_ready, T.t + 1)
                sp.dma_start(u_dram[bass.ds(T.t * P + 2, P), :], u_sb).then_inc(s_u_st, 16)
                sp.wait_ge(s_u_st, (T.t + 1) * 16)
                carry(sp)
                sp.wait_ge(s_conv, T.t * 6)
                sp.dma_start(u1, u_dram[bass.ds(T.t * P + 1, P), :]).then_inc(s_u_ld, 16)
                sp.dma_start(u2, u_dram[bass.ds(T.t * P, P), :]).then_inc(s_u_ld, 16)

            shift_u(Tile(0, 0, 0))
            shift_u(Tile(1, 1, 0))
            sp.wait_ge(s_x1_ready, 1)
            load_x(Tile(2, 0, 1))
            with sp.Fori(0, (NT - 2) // 2 - 1) as i:
                for T in (Tile(2 * i + 1, 1, i), Tile(2 * i + 2, 0, i + 1)):
                    shift_u(T.next())
                    sp.wait_ge(s_x1_ready, T.t + 1)
                    load_x(Tile(T.t + 2, T.par, T.half + 1))
            for T in (Tile(NT - 3, 1, NT // 2 - 2), Tile(NT - 2, 0, NT // 2 - 1)):
                shift_u(T.next())
                if T.t == NT - 3:
                    sp.wait_ge(s_x1_ready, T.t + 1)
                    load_x(Tile(NT - 1, 1, NT // 2 - 1))

            def load_w(slot, gate, up, down):
                w = wts[:, slot * SLOTW:(slot + 1) * SLOTW]
                n = KT * FE
                sp.dma_start(w[:, 0:n], gate.rearrange("(p k) f -> p (k f)", k=KT)).then_inc(w_ld[slot], 16)
                sp.dma_start(w[:, n:2 * n], up.rearrange("(p k) f -> p (k f)", k=KT)).then_inc(w_ld[slot], 16)
                sp.dma_start(w[:, 2 * n:3 * n], down.rearrange("(p k) f -> p (k f)", k=FT)).then_inc(w_ld[slot], 16)

            sp.wait_ge(s_proj, NT * NGR)
            load_w(0, w_sh_gate[0], w_sh_up[0], w_sh_down[0])
            load_w(1, w_exp_gate[0, 0], w_exp_up[0, 0], w_exp_down[0, 0])
            load_w(2, w_exp_gate[0, 1], w_exp_up[0, 1], w_exp_down[0, 1])

            def shared_rows(j, par):
                sp.dma_start(xg[:, par], xn_dram[bass.ds(j * P, P), :]).then_inc(r_ld[par], 16)

            def shared_x1(j, par):
                sp.dma_start(x1l[:, par], x1_dram[bass.ds(j * P, P), :]).then_inc(sh_x1[par], 16)

            sp.wait_ge(s_x1_ready, NT)
            sp.wait_ge(s_xn_st, 16 * (NT - 1))
            shared_rows(0, 0)
            shared_rows(1, 1)
            sp.wait_ge(s_xn_st, 16 * NT)
            sp.wait_ge(s_x1_st, 16 * NT)
            sp.wait_ge(s_pv, NT)
            shared_x1(0, 0)
            shared_x1(1, 1)
            load_w(3, w_exp_gate[0, 2], w_exp_up[0, 2], w_exp_down[0, 2])

            def shared_out(j, par):
                sp.wait_ge(s_y_ready, j + 1)
                sp.dma_start(out2[bass.ds(j * P, P), :], ysb[:, par]).then_inc(sh_st[par], 16)

            for j in range(NSH):
                if j + 2 < NSH:
                    sp.wait_ge(s_xg_t, j + 1)
                    shared_rows(j + 2, j % 2)
                if j >= 1:
                    if 1 < j + 1 < NSH:
                        sp.wait_ge(s_y_ready, j)
                        shared_x1(j + 1, (j + 1) % 2)
                    shared_out(j - 1, (j - 1) % 2)
            shared_out(NSH - 1, (NSH - 1) % 2)

            def load_e(e, slot):
                load_w(slot, w_exp_gate[0, bass.ds(e, 1)].rearrange("a k f -> (a k) f"),
                       w_exp_up[0, bass.ds(e, 1)].rearrange("a k f -> (a k) f"),
                       w_exp_down[0, bass.ds(e, 1)].rearrange("a k f -> (a k) f"))

            sp.wait_ge(s_down, NSH)
            load_e(3, 0)
            sp.wait_ge(s_n_jobs, 4)
            with sp.Fori(0, (NE - NSLOT) // NSLOT) as i:
                for k in range(NSLOT):
                    e = i * NSLOT + NSLOT + k
                    ended_at = sp.value_load(jend_i[0:1, bass.ds(e - NSLOT, 1)], min_val=0, max_val=JMAX)
                    sp.wait_ge(s_down, ended_at + NSH)
                    load_e(e, (k + 1) % NSLOT)
            n = sp.value_load(n_jobs[0:1, 0:1], min_val=MIN_JOBS, max_val=JMAX)
            sp.wait_ge(s_added, n * 16 + 16)
            carry(sp)

        @block.gpsimd
        def _(pool):
            def const(dst, src):
                pool.dma_start(dst, src, allow_slow_non_contiguous=True).then_inc(s_const_ld, 16)

            pool.dma_start(mixw[:, :], mix_norm_w[0].rearrange("(k p) -> p k", p=P),
                           allow_slow_non_contiguous=True).then_inc(s_mixw_ld, 16)
            nc.gpsimd.memset(minus_half[:, :], -0.5).then_inc(s_const_pool, 1)
            nc.gpsimd.memset(ident[:, :], 0.0).then_inc(s_const_pool, 1)
            pool.wait_ge(s_const_pool, 2)
            nc.gpsimd.affine_select(out=ident[:, :], in_=ident[:, :], compare_op=ALU.not_equal, fill=1.0, base=0,
                                    pattern=[[-1, P]], channel_multiplier=1).then_inc(s_const_pool, 1)

            def rsqrt(out_, in_, n, sem_, before):
                pool.wait_ge(sem_, before)
                nc.gpsimd.tensor_tensor(out_, in_, minus_half[:, 0:n], ALU.pow).then_inc(sem_, 1)

            def rsqrt_x(T):
                rsqrt(st_x[:, 2:3], st_x[:, 1:2], 1, s_x_rms, T.t * 2 + 1)

            rsqrt_x(Tile(0, 0, 0))
            const(outw[:, 0:KT // 2], conv_out_norm_w[0].rearrange("(k p) -> p k", p=P))
            const(outw[:, KT // 2:KT], attn_out_norm_w[0].rearrange("(k p) -> p k", p=P))
            for h in range(NKV):
                const(qw[h * HD:(h + 1) * HD, :], q_norm_w[0].rearrange("(p a) -> p a", a=1))
                const(kw[h * HD:(h + 1) * HD, :], k_norm_w[0].rearrange("(p a) -> p a", a=1))
            const(sink[:, :], sinks[0].partition_broadcast(P))
            const(convw[:, :, :].rearrange("p k n -> p (k n)"), conv_w[0].rearrange("k n -> (k n)").partition_broadcast(P))
            const(ffnw[:, :], ffn_norm_w[0].partition_broadcast(P))
            const(rbias[:, :], router_bias[0].partition_broadcast(P))
            const(wr[:, :, :].rearrange("p k n -> p (k n)"), w_router[0].rearrange("(p k) n -> p (k n)", k=KT))

            nc.gpsimd.memset(ones_bf[:, :], 1.0).then_inc(s_const_pool, 1)
            nc.gpsimd.memset(tri_bf[:, :], 1.0).then_inc(s_const_pool, 1)
            nc.gpsimd.memset(upper_bf[:, :], 1.0).then_inc(s_const_pool, 1)
            nc.gpsimd.memset(gtri[:, :, :], 1.0).then_inc(s_const_pool, 1)
            pool.wait_ge(s_const_pool, 7)
            nc.gpsimd.affine_select(out=tri_bf[:, :], in_=tri_bf[:, :], compare_op=ALU.is_gt, fill=0.0, base=0,
                                    pattern=[[1, P]], channel_multiplier=-1).then_inc(s_const_pool, 1)
            nc.gpsimd.affine_select(out=upper_bf[:, 0:NE], in_=upper_bf[:, 0:NE], compare_op=ALU.is_gt, fill=0.0,
                                    base=0, pattern=[[1, NE]], channel_multiplier=-1).then_inc(s_const_pool, 1)
            nc.gpsimd.affine_select(out=upper_bf[:, NE:2 * NE], in_=upper_bf[:, NE:2 * NE], compare_op=ALU.is_ge,
                                    fill=0.0, base=0, pattern=[[1, NE]], channel_multiplier=-1) \
                .then_inc(s_const_pool, 1)
            nc.gpsimd.affine_select(out=gtri[:, :, :], in_=gtri[:, :, :], compare_op=ALU.is_gt, fill=0.0, base=0,
                                    pattern=[[1, NG], [-1, NG]], channel_multiplier=0).then_inc(s_const_pool, 1)
            nc.gpsimd.iota(dist_i, pattern=[[-P, 2], [-1, P]], base=P, channel_multiplier=1) \
                .then_inc(s_const_pool, 1)
            nc.gpsimd.iota(iota_ji, pattern=[[1, JT]], base=0, channel_multiplier=0).then_inc(s_const_pool, 1)
            nc.gpsimd.iota(job_i[:, :, :], pattern=[[0, JT]], base=S, channel_multiplier=1).then_inc(s_const_pool, 1)
            nc.gpsimd.iota(tok_i[:, :, :], pattern=[[P, NT], [0, 8]], base=0, channel_multiplier=1) \
                .then_inc(s_const_pool, 1)

            def store(T):
                pool.wait_ge(s_xn_ready, (T.t + 1) * 3)
                pool.dma_start(xn_dram[bass.ds(T.t * P, P), :], xn).then_inc(s_xn_st, 16)
                pool.dma_start(x1_dram[bass.ds(T.t * P, P), :], x1).then_inc(s_x1_st, 16)

            def rsqrt_qk(T):
                rsqrt(st_q[:, 2, :], st_q[:, 1, :], NH + NKV, s_qk_norm, T.t * 8 + 5)

            def rsqrt_y(T):
                rsqrt(st_y[:, 2, :], st_y[:, 1, :], 2, s_y_rms, T.t * 2 + 1)

            def rsqrt_xn(T):
                rsqrt(st_n[:, 2:3], st_n[:, 1:2], 1, s_xn_ready, T.t * 3 + 1)

            def step(T, first, last):
                N, B = T.next(), T.prev()
                if not last:
                    rsqrt_x(N)
                if not first:
                    rsqrt_xn(B)
                    store(B)
                rsqrt_y(T)
                if not last:
                    rsqrt_qk(N)

            rsqrt_qk(Tile(0, 0, 0))
            front(pool, step)
            rsqrt_xn(Tile(NT - 1, 1, 0))
            store(Tile(NT - 1, 1, 0))

            pool.wait_ge(s_init_st, 32)
            for t in range(NT):
                pool.wait_ge(s_post_idx, 6 * (t + 1))
                for j in range(8):
                    n = t * 8 + j
                    pool.indirect_dma_start(out=table[:, :],
                                            out_offset=bass.IndirectOffsetOnAxis(ap=slot_i[:, n:n + 1], axis=0),
                                            in_=pay[:, t, j, :], in_offset=None).then_inc(s_sc_tab, 16)

            pool.wait_ge(s_sc_tab, 16 * NT * 8)
            pool.dma_start(tab[:, :, :], table.rearrange("(p j) c -> p j c", p=P)).then_inc(s_added, 16)
            tab_i = tab[:, :, :].bitcast(I32)

            def gather(j, par, copies):
                pool.wait_ge(s_xg_t, j - 1)
                nc.gpsimd.tensor_copy(gidx[:, par:par + 1], tab_i[:, bass.ds(j - NSH, 1), 0:1]
                                      .rearrange("p a b -> p (a b)")).then_inc(s_idx_cp, 1)
                pool.wait_ge(s_idx_cp, copies + 1)
                carry(pool)
                pool.indirect_dma_start(out=xg[:, par], out_offset=None, in_=xn_dram[:, :],
                                        in_offset=bass.IndirectOffsetOnAxis(ap=gidx[:, par:par + 1], axis=0),
                                        bounds_check=S - 1, oob_is_err=False).then_inc(g_ld[par], 16)

            def scatter(j, par, copies):
                nc.gpsimd.tensor_copy(sidx[:, par:par + 1], tab_i[:, bass.ds(j - NSH, 1), 0:1]
                                      .rearrange("p a b -> p (a b)")).then_inc(s_idx_cp, 1)
                pool.wait_ge(s_idx_cp, copies + 1)
                pool.wait_ge(s_y_ready, j + 1)
                pool.wait_ge(s_added, (j - (NSH - 1)) * 16)
                carry(pool)
                pool.indirect_dma_start(out=out2[:, :],
                                        out_offset=bass.IndirectOffsetOnAxis(ap=sidx[:, par:par + 1], axis=0),
                                        in_=ysb[:, par], in_offset=None, bounds_check=S - 1,
                                        oob_is_err=False, compute_op=ALU.add).then_inc(s_added, 16)

            pool.wait_ge(s_added, 16)
            gather(NSH, 0, 0)
            gather(NSH + 1, 1, 1)
            gather(NSH + 2, 0, 2)
            for b in range(2):
                pool.wait_ge(sh_st[b], 8 * NSH)
            pool.wait_ge(s_n_jobs, 4)
            n = pool.value_load(n_jobs[0:1, 0:1], min_val=MIN_JOBS, max_val=JMAX)

            def jobs(i, ks):
                for k in ks:
                    j = i * 2 + (NSH + k)
                    gather(j + 3, 1 - k, i * 4 + (3 + 2 * k))
                    scatter(j, k, i * 4 + (4 + 2 * k))

            routed_jobs(pool, 0, jobs)
            pool.wait_ge(g_ld[0], ((n + 4) // 2) * 16)
            pool.wait_ge(g_ld[1], ((n + 3) // 2) * 16)
            pool.wait_ge(s_added, n * 16 + 16)

        @block.tensor
        def _(pe):
            def mm(out_, lhsT, rhs, start, stop):
                return nc.tensor.matmul(out_, lhsT, rhs, start=start, stop=stop)

            def t_x(T):
                pe.wait_ge(s_x_scaled, T.t + 1)
                for k in range(KT):
                    i = nc.tensor.transpose(psT[:, k, :], xs[:, k * P:(k + 1) * P], ident[:, :])
                i.then_inc(s_tx, 1)

            def project(T, g):
                _, c0, n = GROUPS[g]
                bank = (NGR * T.par + g) % 2
                if g == 0:
                    pe.wait_ge(s_uT_ready, T.t + 1)
                if not (isinstance(T.t, int) and T.t == 0 and g < 2):
                    pe.wait_ge(s_proj_out, T.t * NGR + (g - 1))
                for k in range(KT):
                    i = mm(psP[:, bank, 0:n], uT[:, k, :], w_in_sb[:, k, c0:c0 + n], k == 0, k == KT - 1)
                i.then_inc(s_proj, 1)

            def t_qk(T):
                pe.wait_ge(s_qk_norm, (T.t + 1) * 8)
                for hp in range(HP):
                    nc.tensor.transpose(psT[:, hp, :], qn[:, hp * P:(hp + 1) * P], ident[:, :])
                nc.tensor.transpose(psT[:, HP, :], kn[:, :], ident[:, :]).then_inc(s_tqk, 1)

            def scores(T, first):
                pe.wait_ge(s_qkT, (T.t + 1) * 2)
                if not first:
                    pe.wait_ge(s_x1_ready, T.t)
                for kv in range(NKV):
                    r = slice(kv * HD, (kv + 1) * HD)
                    for hp in range(HP):
                        h = kv * HP + hp
                        o = psW[:, h // 2, (h % 2) * 2 * P:(h % 2 + 1) * 2 * P]
                        if not first:
                            mm(o[:, 0:P], qT[r, hp, :], kT[r, 1 - T.par, :], True, True)
                        i = mm(o[:, P:2 * P], qT[r, hp, :], kT[r, T.par, :], True, True)
                i.then_inc(s_scores, 1)

            def t_p(T, first):
                pe.wait_ge(s_exps, (T.t + 1) * 9)
                for h in range(NH):
                    for half in range(1 if first else 0, 2):
                        n = h * 2 + half
                        i = nc.tensor.transpose(psW[:, n // 4, (n % 4) * P:(n % 4 + 1) * P],
                                                s_sb[:, h, half * P:(half + 1) * P], ident[:, :])
                i.then_inc(s_pt, 1)

            def p_v(T, first):
                pe.wait_ge(s_pT_ready, T.t + 1)
                for h in range(NH):
                    v = slice(DKV + (h // HP) * HD, DKV + (h // HP + 1) * HD)
                    o = psW[:, 0, h * HD:(h + 1) * HD]
                    if not first:
                        mm(o, pT[:, 2 * h, :], kv_sb[:, 1 - T.par, v], True, False)
                    i = mm(o, pT[:, 2 * h + 1, :], kv_sb[:, T.par, v], first, True)
                i.then_inc(s_pv, 1)

            def t_y(T):
                pe.wait_ge(s_y_scaled, (T.t + 1) * 2)
                for k in range(KT):
                    i = nc.tensor.transpose(psT[:, k, :], ys[:, k * P:(k + 1) * P], ident[:, :])
                i.then_inc(s_ty, 1)

            def out_project(T, n):
                if n == 0:
                    pe.wait_ge(s_yT_ready, T.t + 1)
                for k in range(KT):
                    i = mm(psW[:, 2 + n, :], yT[:, k, :], w_out_sb[:, k, n * 512:(n + 1) * 512], k == 0, k == KT - 1)
                if n == 1:
                    i.then_inc(s_outproj, 1)

            def t_xn(T):
                pe.wait_ge(s_xn_ready, (T.t + 1) * 3)
                for k in range(KT):
                    i = nc.tensor.transpose(psT[:, k, :], xn[:, k * P:(k + 1) * P], ident[:, :])
                i.then_inc(s_txn, 1)

            def router(T):
                pe.wait_ge(s_xnT_ready, T.t + 1)
                for k in range(KT):
                    i = mm(psW[:, 1, 0:NE], xnT[:, k, :], wr[:, k, :], k == 0, k == KT - 1)
                i.then_inc(s_logits, 1)

            def position(T):
                pe.wait_ge(s_route, (T.t + 1) * N_RT)
                mm(psW[:, 1, 0:NE], ones_bf[:, :], msum[:, bass.ds(T.t, 1), :].rearrange("p a e -> p (a e)"),
                   True, False)
                mm(psW[:, 1, 0:NE], tri_bf[:, :], m_all[:, bass.ds(T.t, 1), :].rearrange("p a e -> p (a e)"),
                   False, True).then_inc(s_position, 1)

            def step(T, first, last):
                N, B = T.next(), T.prev()
                scores(T, first)
                if not last:
                    pe.wait_ge(s_qkT, (T.t + 1) * 2)
                    t_x(N)
                    project(N, 0)
                    project(N, 1)
                if not first:
                    if not last:
                        pe.wait_ge(s_uT_ready, N.t + 1)
                    t_xn(B)
                t_p(T, first)
                if not last:
                    project(N, 2)
                p_v(T, first)
                if not first:
                    router(B)
                if not last:
                    project(N, 3)
                if not first:
                    pe.wait_ge(s_xnT_ready, B.t + 1)
                else:
                    pe.wait_ge(s_uT_ready, N.t + 1)
                t_y(T)
                if not last:
                    project(N, 4)
                if not first:
                    position(B)
                if first:
                    pe.wait_ge(s_wout_ld, 16)
                out_project(T, 0)
                if not last:
                    t_qk(N)
                out_project(T, 1)

            GUW = KT * FE

            def t_job(j, par, loads, nth):
                pe.wait_ge(loads[par], nth * 16)
                if not (isinstance(j, int) and j == 0):
                    pe.wait_ge(s_xT_ready, j)
                for k in range(KT):
                    i = nc.tensor.transpose(psT[:, k, :], xg[:, par, k * P:(k + 1) * P], ident[:, :])
                i.then_inc(s_xg_t, 1)

            def gate_up(j, par, w0, ks=range(KT)):
                if 0 in ks:
                    pe.wait_ge(s_xT_ready, j + 1)
                    if not isinstance(j, int) or j >= 2:
                        pe.wait_ge(s_h_ready, j - 1)
                for k in ks:
                    if isinstance(w0, int):
                        w = wts[:, w0:w0 + 2 * GUW]
                    else:
                        w = wts[:, bass.ds(w0, 2 * GUW)]
                    rhs = w.rearrange("p (m k f) -> p m k f", m=2, k=KT)[:, :, k, :]
                    i = mm(psP[:, par, :].rearrange("p (m f) -> p m f", m=2), xT[:, k, :], rhs, k == 0, k == KT - 1)
                if KT - 1 in ks:
                    i.then_inc(s_gu, 1)

            def t_h(j):
                pe.wait_ge(s_h_ready, j + 1)
                for f in range(FT):
                    i = nc.tensor.transpose(psW[:, 0, f * P:(f + 1) * P], hh[:, f * P:(f + 1) * P], ident[:, :])
                i.then_inc(s_th, 1)

            def down(j, w0):
                pe.wait_ge(s_hT_ready, j + 1)
                if not (isinstance(j, int) and j == 0):
                    pe.wait_ge(s_y_ready, j)
                for n in range(2):
                    for f in range(FT):
                        o = 2 * GUW + f * D + n * 512
                        rhs = wts[:, w0 + o:w0 + o + 512] if isinstance(w0, int) else wts[:, bass.ds(w0 + o, 512)]
                        i = mm(psW[:, 2 + n, :], hT[:, f, :], rhs, f == 0, f == FT - 1)
                i.then_inc(s_down, 1)

            pe.wait_ge(s_const_pool, 3)
            T0 = Tile(0, 0, 0)
            t_x(T0)
            for g in range(NGR):
                pe.wait_ge(win_ld[g], 16)
                project(T0, g)
            t_qk(T0)
            pe.wait_ge(s_const_ld, 16 * N_CONST)
            front(pe, step)
            TL = Tile(NT - 1, 1, NT // 2 - 1)
            t_xn(TL)
            router(TL)
            pe.wait_ge(s_xnT_ready, NT)
            t_job(0, 0, r_ld, 1)
            pe.wait_ge(s_proj_out, NT * NGR)
            pe.wait_ge(w_ld[0], 48)
            gate_up(0, 0, 0, range(0, 2))
            position(TL)
            gate_up(0, 0, 0, range(2, 3))
            pe.wait_ge(s_pos_ready, NT)
            mm(psW[0:NE, 1, 0:1], msum[:, NT, :], ones_bf[:, 0:1], True, True).then_inc(s_pre_pe, 1)
            gate_up(0, 0, 0, range(3, 5))
            pe.wait_ge(s_post, 4)
            mm(psW[:, 0, 0:2 * NE], nb_row[:, :], upper_bf[:, :], True, True)
            mm(psW[0:NE, 0, 2 * NE:2 * NE + 1], upper_bf[:, NE:2 * NE], nb_bf[:, :], True, True) \
                .then_inc(s_post_pe, 1)
            gate_up(0, 0, 0, range(5, 6))
            pe.wait_ge(s_post, 6)
            mm(psW[:, 1, 0:JT], ones_bf[0:NE, :], ended[:, :], True, True).then_inc(s_post_pe, 1)
            gate_up(0, 0, 0, range(6, KT))

            t_job(1, 1, r_ld, 1)
            gate_up(1, 1, 0)
            pe.wait_ge(s_post, 7)
            t_h(0)
            for j in range(1, NSH):
                if j >= 2:
                    gate_up(j, j % 2, 0)
                if j + 1 < NSH:
                    t_job(j + 1, (j + 1) % 2, r_ld, (j + 1) // 2 + 1)
                else:
                    t_job(NSH, 0, g_ld, 1)
                down(j - 1, 0)
                t_h(j)
            pe.wait_ge(s_n_jobs, 4)
            n = pe.value_load(n_jobs[0:1, 0:1], min_val=MIN_JOBS, max_val=JMAX)

            def jobs(i, ks):
                for k in ks:
                    r = i * 2 + k
                    was = pe.value_load(ring_i[0:1, bass.ds(r, 1)], min_val=0, max_val=NE)
                    now = pe.value_load(ring_i[0:1, bass.ds(r + 1, 1)], min_val=1, max_val=NE)
                    for sl in range(NSLOT):
                        loads = (now + (NSLOT - sl)) // NSLOT
                        pe.wait_ge(w_ld[sl], (loads + (1 >> loads)) * 48)
                    gate_up(r + NSH, k, (now % NSLOT) * SLOTW)
                    t_job(r + NSH + 1, 1 - k, g_ld, i + (1 + k))
                    down(r + NSH - 1, (was % NSLOT) * SLOTW)
                    t_h(r + NSH)

            routed_jobs(pe, 0, jobs)
            last = pe.value_load(ring_i[0:1, bass.ds(n, 1)], min_val=0, max_val=NE)
            down(n + (NSH - 1), (last % NSLOT) * SLOTW)

        @block.scalar
        def _(act):
            A = nc.scalar.activation

            def x_square(T):
                act.wait_ge(x_ld[T.par], (T.half + 1) * 16)
                A(junk[:, :], x_sb[:, T.par], ACT.Square, accum_out=st_x[:, 0:1]).then_inc(s_x_sq, 1)

            def x_scale(T):
                act.wait_ge(s_x_rms, (T.t + 1) * 2)
                if not isinstance(T.t, int) or T.t >= 1:
                    act.wait_ge(s_tx, T.t)
                A(xs, x_sb[:, T.par], ACT.Copy, scale=st_x[:, 2:3]).then_inc(s_x_scaled, 1)

            def read_group(T, g):
                name, _, n = GROUPS[g]
                bank = (NGR * T.par + g) % 2
                dst = {"c": c_sb, "h": h_sb, "b": b_sb, "q": q_sb}.get(name)
                if name == "kv":
                    dst = kv_sb[:, T.par, :]
                zero = isinstance(T.t, int) and T.t == 0
                if not zero:
                    if name == "c":
                        act.wait_ge(s_conv, T.t * 6)
                        act.wait_ge(s_u_st, T.t * 16)
                    if name == "h":
                        act.wait_ge(s_u_ready, T.t)
                    if name == "b":
                        act.wait_ge(s_conv, T.t * 6)
                    if name in "qkv":
                        act.wait_ge(s_qk_norm, T.t * 8)
                    if name == "kv":
                        act.wait_ge(s_pv, T.t)
                act.wait_ge(s_proj, T.t * NGR + g + 1)
                A(dst, psP[:, bank, 0:n], ACT.Copy).then_inc(s_proj_out, 1)

            def read_qk(T, first):
                act.wait_ge(s_tqk, T.t + 1)
                if not first:
                    act.wait_ge(s_scores, T.t)
                A(qT[:, :, :], psT[:, 0:HP, :], ACT.Copy, scale=qw[:, 0:1]).then_inc(s_qkT, 1)
                A(kT[:, T.par, :], psT[:, HP, :], ACT.Copy, scale=kw[:, 0:1]).then_inc(s_qkT, 1)

            def exps(T, first):
                a = P if first else 0
                act.wait_ge(s_soft, (T.t + 1) * 5)
                for h in range(NH):
                    A(s_sb[:, h, a:2 * P], s_sb[:, h, a:2 * P], ACT.Exp, bias=st_s[:, 2, h:h + 1],
                      accum_out=st_s[:, 4, h:h + 1]).then_inc(s_exps, 1)
                A(st_s[:, 5, :], st_s[:, 3, :], ACT.Exp).then_inc(s_exps, 1)

            def read_p(T, first):
                act.wait_ge(s_pt, T.t + 1)
                if first:
                    act.wait_ge(s_init_st, 32)
                    act.wait_ge(s_const_dve, 11 + NH)
                    A(pT[:, :, :].rearrange("p (h a) k -> p h a k", a=2)[:, :, 1, :],
                      psW[:, :, :].rearrange("p b (a c k) -> p (b a) c k", a=2, c=2)[:, :, 1, :], ACT.Copy) \
                        .then_inc(s_pT_ready, 1)
                else:
                    act.wait_ge(s_pv, T.t)
                    A(pT.rearrange("p h k -> p (h k)"), psW[:, :, :].rearrange("p b n -> p (b n)"), ACT.Copy) \
                        .then_inc(s_pT_ready, 1)

            def y_square(T):
                act.wait_ge(s_conv, (T.t + 1) * 6)
                A(junk[:, 0:DC], y_conv, ACT.Square, accum_out=st_y[:, 0, 0:1]).then_inc(s_y_sq, 1)
                act.wait_ge(s_o_norm, (T.t + 1) * 3)
                A(junk[:, DC:2 * DC], y_attn, ACT.Square, accum_out=st_y[:, 0, 1:2]).then_inc(s_y_sq, 1)

            def y_scale(T, first):
                act.wait_ge(s_y_rms, (T.t + 1) * 2)
                if not first:
                    act.wait_ge(s_xn_ready, T.t * 3)
                    act.wait_ge(s_x1_st, T.t * 16)
                    act.wait_ge(s_txn, T.t)
                    act.wait_ge(s_xn_st, T.t * 16)
                A(ys[:, 0:DC], y_conv, ACT.Copy, scale=st_y[:, 2, 0:1]).then_inc(s_y_scaled, 1)
                A(ys[:, DC:2 * DC], y_attn, ACT.Copy, scale=st_y[:, 2, 1:2]).then_inc(s_y_scaled, 1)

            def x1_square(T):
                act.wait_ge(s_x1_ready, T.t + 1)
                A(junk[:, :], x1, ACT.Square, accum_out=st_n[:, 0:1]).then_inc(s_x1_sq, 1)

            def read_xn(T):
                act.wait_ge(s_txn, T.t + 1)
                act.wait_ge(s_outproj, T.t + 1)
                A(xnT, psT[:, :, :], ACT.Copy).then_inc(s_xnT_ready, 1)

            def sigmoid(T):
                act.wait_ge(s_logits, T.t + 1)
                act.wait_ge(s_yT_ready, T.t + 1)
                A(sc[:, :], psW[:, 1, 0:NE], ACT.Sigmoid).then_inc(s_sigm, 1)

            def step(T, first, last):
                N, B = T.next(), T.prev()
                if not last:
                    act.wait_ge(s_x1_sq, T.t)
                    x_square(N)
                if not last:
                    x_scale(N)
                exps(T, first)
                if not last:
                    read_group(N, 0)
                    read_group(N, 1)
                if not first:
                    read_xn(B)
                read_p(T, first)
                if not last:
                    read_group(N, 2)
                if not first:
                    sigmoid(B)
                y_square(T)
                y_scale(T, first)
                if not last:
                    read_group(N, 3)
                    read_group(N, 4)
                    read_qk(N, False)
                x1_square(T)

            T0 = Tile(0, 0, 0)
            x_square(T0)
            x_scale(T0)
            for g in range(NGR):
                read_group(T0, g)
            act.wait_ge(s_const_ld, 16 * N_CONST)
            read_qk(T0, True)
            front(act, step)
            TL = Tile(NT - 1, 1, NT // 2 - 1)
            read_xn(TL)
            sigmoid(TL)

            def silu(j, par):
                act.wait_ge(s_gu, j + 1)
                if not (isinstance(j, int) and j == 0):
                    act.wait_ge(s_h_ready, j)
                A(sg, psP[:, par, 0:FE], ACT.Silu).then_inc(s_silu, 1)

            def read_h(j):
                act.wait_ge(s_th, j + 1)
                if not (isinstance(j, int) and j == 0):
                    act.wait_ge(s_down, j)
                A(hT.rearrange("p f n -> p (f n)"), psW[:, 0, 0:FE], ACT.Copy).then_inc(s_hT_ready, 1)

            def read_y(j, par, static):
                act.wait_ge(s_down, j + 1)
                if static:
                    act.wait_ge(sh_st[0], 8 * NSH)
                    act.wait_ge(sh_st[1], 8 * NSH)
                else:
                    act.wait_ge(s_added, (j - NSH) * 16)
                A(ysb[:, par], psW[:, 2:4, :].rearrange("p a n -> p (a n)"), ACT.Copy).then_inc(s_y_ready, 1)

            act.wait_ge(s_y_sq, 2 * NT)
            for j in range(NSH):
                silu(j, j % 2)
                read_h(j)
            act.wait_ge(s_n_jobs, 4)
            n_less_2 = act.value_load(n_jobs[0:1, 1:2], min_val=MIN_JOBS - 2, max_val=JMAX - 2)
            silu(NSH, 0)
            read_h(NSH)
            silu(NSH + 1, 1)
            read_y(NSH, 0, True)
            read_h(NSH + 1)

            def jobs(i, ks):
                for k in ks:
                    j = i * 2 + (NSH + 2 + k)
                    silu(j, k)
                    read_y(j - 1, 1 - k, False)
                    read_h(j)

            one = routed_jobs(act, 1, jobs)
            with act.If_ne(one, 0):
                read_y(n_less_2 + (NSH + 1), 0, False)
            with act.If_eq(one, 0):
                read_y(n_less_2 + (NSH + 1), 1, False)

        @block.vector
        def _(dve):
            V = nc.vector

            def mean_eps(tmp, src, n, sem_):
                V.tensor_scalar(tmp, src, 1.0 / n, EPS, ALU.mult, ALU.add).then_inc(sem_, 1)

            def constants():
                dve.wait_ge(s_const_pool, 15)
                V.memset(one_col[:, :], 1.0).then_inc(s_const_dve, 1)
                V.memset(zrow[:, :], 0.0).then_inc(s_const_dve, 1)
                V.memset(msum[:, 0, :], 0.0).then_inc(s_const_dve, 1)
                V.memset(job0[:, :, :], 0.0).then_inc(s_const_dve, 1)
                V.tensor_copy(iota_j[:, :], iota_ji).then_inc(s_const_dve, 1)
                dve.wait_ge(s_const_dve, 5)
                V.tensor_copy(job0[:, :, 0:1].bitcast(I32), job_i[:, :, :]).then_inc(s_const_dve, 1)
                V.tensor_copy(pay[:, :, :, 0:1].bitcast(I32).rearrange("p t j a -> p t (j a)"), tok_i[:, :, :]) \
                 .then_inc(s_const_dve, 1)
                V.tensor_copy(dist, dist_i).then_inc(s_const_dve, 1)
                dve.wait_ge(s_const_dve, 8)
                V.tensor_scalar(far, dist, 0.0, -BIG, ALU.is_lt, ALU.mult).then_inc(s_const_dve, 1)
                V.tensor_scalar(far_b, dist, float(P), -BIG, ALU.is_ge, ALU.mult).then_inc(s_const_dve, 1)
                dve.wait_ge(s_const_dve, 10)
                V.tensor_tensor(far, far, far_b, ALU.add).then_inc(s_const_dve, 1)
                dve.wait_ge(s_const_dve, 11)
                for h in range(NH):
                    V.scalar_tensor_tensor(out=bias[:, h, :], in0=dist, scalar=-(2.0 ** (-8.0 * (h + 1) / NH)),
                                           in1=far, op0=ALU.mult, op1=ALU.add).then_inc(s_const_dve, 1)
                dve.wait_ge(s_const_dve, 11 + NH)
                dve.wait_ge(s_const_ld, 16 * N_CONST)

            def x_rms(T):
                dve.wait_ge(s_x_sq, T.t + 1)
                mean_eps(st_x[:, 1:2], st_x[:, 0:1], D, s_x_rms)

            def read_uT(T):
                dve.wait_ge(s_tx, T.t + 1)
                if not (isinstance(T.t, int) and T.t == 0):
                    dve.wait_ge(s_proj, T.t * NGR)
                V.tensor_tensor(uT, psT[:, :, :], bc(mixw[:, :].unsqueeze(2), [P, KT, P]), ALU.mult) \
                 .then_inc(s_uT_ready, 1)

            def u_mul(T):
                dve.wait_ge(s_proj_out, T.t * NGR + 2)
                V.tensor_tensor(u_sb, c_sb, h_sb, ALU.mult).then_inc(s_u_ready, 1)

            def conv(T):
                dve.wait_ge(s_u_ld, (T.t + 1) * 32)
                dve.wait_ge(s_u_ready, T.t + 1)
                dve.wait_ge(s_proj_out, T.t * NGR + 3)
                b = T.t * 6
                V.tensor_tensor(u2, u2, convw[:, 0, :], ALU.mult).then_inc(s_conv, 1)
                V.tensor_tensor(u1, u1, convw[:, 1, :], ALU.mult).then_inc(s_conv, 1)
                dve.wait_ge(s_conv, b + 2)
                V.tensor_tensor(u2, u2, u1, ALU.add).then_inc(s_conv, 1)
                dve.wait_ge(s_conv, b + 3)
                V.tensor_tensor(u1, u_sb, convw[:, 2, :], ALU.mult).then_inc(s_conv, 1)
                dve.wait_ge(s_conv, b + 4)
                V.tensor_tensor(u2, u2, u1, ALU.add).then_inc(s_conv, 1)
                dve.wait_ge(s_conv, b + 5)
                if not (isinstance(T.t, int) and T.t == 0):
                    dve.wait_ge(s_y_scaled, T.t * 2)
                V.tensor_tensor(y_conv, u2, b_sb, ALU.mult).then_inc(s_conv, 1)

            def qk_norm(T):
                k = kv_sb[:, T.par, 0:DKV]
                b = T.t * 8
                dve.wait_ge(s_proj_out, T.t * NGR + NGR)
                if not (isinstance(T.t, int) and T.t == 0):
                    dve.wait_ge(s_tqk, T.t)
                V.tensor_tensor(dsq[:, :], q_sb, q_sb, ALU.mult).then_inc(s_qk_norm, 1)
                dve.wait_ge(s_qk_norm, b + 1)
                V.tensor_reduce(st_q[:, 0, 0:NH], dsq[:, :].rearrange("p (h d) -> p h d", h=NH), AX.X, ALU.add) \
                 .then_inc(s_qk_norm, 1)
                dve.wait_ge(s_qk_norm, b + 2)
                V.tensor_tensor(dsq[:, 0:DKV], k, k, ALU.mult).then_inc(s_qk_norm, 1)
                dve.wait_ge(s_qk_norm, b + 3)
                V.tensor_reduce(st_q[:, 0, NH:NH + NKV], dsq[:, 0:DKV].rearrange("p (h d) -> p h d", h=NKV), AX.X,
                                ALU.add).then_inc(s_qk_norm, 1)
                dve.wait_ge(s_qk_norm, b + 4)
                mean_eps(st_q[:, 1, :], st_q[:, 0, :], HD, s_qk_norm)
                dve.wait_ge(s_qk_norm, b + 6)
                V.tensor_tensor(qn.rearrange("p (h v d) -> p v h d", h=HP, v=NKV),
                                q_sb.rearrange("p (v h d) -> p v h d", h=HP, v=NKV),
                                bc(st_q[:, 2, 0:NH].rearrange("p (v h) -> p v h", v=NKV).unsqueeze(3),
                                   [P, NKV, HP, HD]), ALU.mult).then_inc(s_qk_norm, 1)
                V.tensor_tensor(kn[:, :].rearrange("p (h d) -> p h d", h=NKV), k.rearrange("p (h d) -> p h d", h=NKV),
                                bc(st_q[:, 2, NH:NH + NKV].unsqueeze(2), [P, NKV, HD]), ALU.mult) \
                 .then_inc(s_qk_norm, 1)

            def soft_a(T, first):
                a = P if first else 0
                dve.wait_ge(s_scores, T.t + 1)
                if not first:
                    dve.wait_ge(s_pt, T.t)
                V.scalar_tensor_tensor(out=s_sb[:, :, a:2 * P],
                                       in0=psW[:, :, :].rearrange("p b (c k) -> p (b c) k", c=2)[:, :, a:2 * P],
                                       scalar=float(HD) ** -0.5, in1=bias[:, :, a:2 * P], op0=ALU.mult,
                                       op1=ALU.add).then_inc(s_soft, 1)

            def soft_b(T, first):
                a = P if first else 0
                b = T.t * 5
                dve.wait_ge(s_soft, b + 1)
                V.tensor_reduce(st_s[:, 0, :], s_sb[:, :, a:2 * P], AX.X, ALU.max).then_inc(s_soft, 1)
                dve.wait_ge(s_soft, b + 2)
                V.tensor_tensor(st_s[:, 1, :], st_s[:, 0, :], sink[:, :], ALU.max).then_inc(s_soft, 1)
                dve.wait_ge(s_soft, b + 3)
                V.tensor_scalar(st_s[:, 2, :], st_s[:, 1, :], -1.0, None, ALU.mult).then_inc(s_soft, 1)
                V.tensor_tensor(st_s[:, 3, :], sink[:, :], st_s[:, 1, :], ALU.subtract).then_inc(s_soft, 1)

            def o_norm(T):
                b = T.t * 3
                dve.wait_ge(s_exps, (T.t + 1) * 9)
                V.tensor_tensor(st_s[:, 6, :], st_s[:, 4, :], st_s[:, 5, :], ALU.add).then_inc(s_o_norm, 1)
                dve.wait_ge(s_o_norm, b + 1)
                V.reciprocal(st_s[:, 7, :], st_s[:, 6, :]).then_inc(s_o_norm, 1)
                dve.wait_ge(s_o_norm, b + 2)
                dve.wait_ge(s_pv, T.t + 1)
                if not (isinstance(T.t, int) and T.t == 0):
                    dve.wait_ge(s_y_scaled, T.t * 2)
                V.tensor_tensor(y_attn.rearrange("p (h d) -> p h d", h=NH),
                                psW[:, 0, :].rearrange("p (h d) -> p h d", h=NH),
                                bc(st_s[:, 7, :].unsqueeze(2), [P, NH, HD]), ALU.mult).then_inc(s_o_norm, 1)

            def y_rms(T):
                dve.wait_ge(s_y_sq, (T.t + 1) * 2)
                mean_eps(st_y[:, 1, :], st_y[:, 0, :], DC, s_y_rms)

            def read_yT(T):
                dve.wait_ge(s_ty, T.t + 1)
                if not (isinstance(T.t, int) and T.t == 0):
                    dve.wait_ge(s_logits, T.t)
                V.tensor_tensor(yT, psT[:, :, :], bc(outw[:, :].unsqueeze(2), [P, KT, P]), ALU.mult) \
                 .then_inc(s_yT_ready, 1)

            def x1_add(T):
                dve.wait_ge(s_outproj, T.t + 1)
                V.tensor_tensor(x1, psW[:, 2:4, :].rearrange("p a n -> p (a n)"), x_sb[:, T.par], ALU.add) \
                 .then_inc(s_x1_ready, 1)

            def xn_make(T):
                dve.wait_ge(s_x1_sq, T.t + 1)
                dve.wait_ge(s_tx, T.t + 3 if not isinstance(T.t, int) or T.t <= NT - 3 else NT)
                mean_eps(st_n[:, 1:2], st_n[:, 0:1], D, s_xn_ready)
                dve.wait_ge(s_xn_ready, T.t * 3 + 2)
                V.scalar_tensor_tensor(out=xn.rearrange("t (k p) -> t p k", k=KT),
                                       in0=x1.rearrange("t (p k) -> t p k", k=KT), scalar=st_n[:, 2:3],
                                       in1=ffnw[:, :].rearrange("t (p k) -> t p k", k=KT), op0=ALU.mult,
                                       op1=ALU.mult).then_inc(s_xn_ready, 1)

            def route(T):
                b = T.t * N_RT
                n = [0]

                def done(i, wait=True):
                    i.then_inc(s_route, 1)
                    n[0] += 1
                    if wait:
                        dve.wait_ge(s_route, b + n[0])

                dve.wait_ge(s_sigm, T.t + 1)
                done(V.tensor_tensor(bi[:, :], sc[:, :], rbias[:, :], ALU.add))
                carry(dve)
                for g in range(NG):
                    done(V.max(g8[:, g, :], bi[:, g * EG:(g + 1) * EG]), g == NG - 1)
                done(V.tensor_tensor(gs[:, :], g8[:, :, 0], g8[:, :, 1], ALU.add))
                gi = bc(gs[:, :].unsqueeze(2), [P, NG, NG])
                gj = bc(gs[:, :].unsqueeze(1), [P, NG, NG])
                done(V.tensor_tensor(gcmp[:, :, :], gj, gi, ALU.is_gt), False)
                done(V.tensor_tensor(geq[:, :, :], gj, gi, ALU.is_equal))
                done(V.tensor_tensor(geq[:, :, :], geq[:, :, :], gtri[:, :, :], ALU.mult))
                done(V.tensor_tensor(gcmp[:, :, :], gcmp[:, :, :], geq[:, :, :], ALU.add))
                done(V.tensor_reduce(rank[:, :], gcmp[:, :, :], AX.X, ALU.add))
                done(V.tensor_scalar(rank[:, :], rank[:, :], TOPG - 0.5, -BIG, ALU.is_gt, ALU.mult))
                done(V.tensor_tensor(mb[:, :].rearrange("p (g e) -> p g e", g=NG),
                                     bi[:, :].rearrange("p (g e) -> p g e", g=NG),
                                     bc(rank[:, :].unsqueeze(2), [P, NG, EG]), ALU.add))
                carry(dve)
                done(V.max(top[:, :], mb[:, :]))
                carry(dve)
                done(V.match_replace(mr[:, :], top[:, :], mb[:, :], -3e38))
                m = m_all[:, bass.ds(T.t, 1), :].rearrange("p a e -> p (a e)")
                w = w_all[:, bass.ds(T.t, 1), :].rearrange("p a e -> p (a e)")
                done(V.tensor_scalar(m, mr[:, :], -2e38, None, ALU.is_lt))
                done(V.tensor_tensor(msum[:, bass.ds(T.t + 1, 1), :].rearrange("p a e -> p (a e)"), m,
                                     msum[:, bass.ds(T.t, 1), :].rearrange("p a e -> p (a e)"), ALU.add), False)
                done(V.tensor_tensor(mb[:, :], sc[:, :], m, ALU.mult))
                done(V.tensor_reduce(wsum[:, 0:1], mb[:, :], AX.X, ALU.add))
                done(V.reciprocal(wsum[:, 1:2], wsum[:, 0:1]))
                V.tensor_scalar(w, mb[:, :], wsum[:, 1:2], SCALE_ROUTED, ALU.mult, ALU.mult).then_inc(s_route, 1)
                n[0] += 1
                assert n[0] == N_RT, n[0]

            def read_pos(T):
                dve.wait_ge(s_position, T.t + 1)
                V.tensor_copy(pos[:, bass.ds(T.t, 1), :].rearrange("p a e -> p (a e)"), psW[:, 1, 0:NE]) \
                 .then_inc(s_pos_ready, 1)

            def step(T, first, last):
                N, B = T.next(), T.prev()
                if not last:
                    x_rms(N)
                if not last:
                    read_uT(N)
                soft_a(T, first)
                soft_b(T, first)
                if not first:
                    xn_make(B)
                if not last:
                    u_mul(N)
                o_norm(T)
                y_rms(T)
                if not first:
                    route(B)
                read_yT(T)
                if not first:
                    read_pos(B)
                if not last:
                    qk_norm(N)
                    conv(N)
                x1_add(T)

            T0 = Tile(0, 0, 0)
            x_rms(T0)
            dve.wait_ge(s_mixw_ld, 16)
            read_uT(T0)
            constants()
            u_mul(T0)
            qk_norm(T0)
            conv(T0)
            def read_xT(j):
                dve.wait_ge(s_xg_t, j + 1)
                if not (isinstance(j, int) and j == 0):
                    dve.wait_ge(s_gu, j)
                V.tensor_copy(xT, psT[:, :, :]).then_inc(s_xT_ready, 1)

            def h_mul(j, par, w):
                dve.wait_ge(s_silu, j + 1)
                if not (isinstance(j, int) and j == 0):
                    dve.wait_ge(s_th, j)
                V.scalar_tensor_tensor(out=hh.rearrange("t (f p) -> t p f", f=FT),
                                       in0=sg.rearrange("t (p f) -> t p f", f=FT), scalar=w,
                                       in1=psP[:, par, FE:2 * FE].rearrange("t (p f) -> t p f", f=FT),
                                       op0=ALU.mult, op1=ALU.mult).then_inc(s_h_ready, 1)

            front(dve, step)
            TL = Tile(NT - 1, 1, NT // 2 - 1)
            xn_make(TL)
            dve.wait_ge(s_xn_st, 16 * NT)
            read_xT(0)
            route(TL)
            read_pos(TL)

            dve.wait_ge(s_pre_pe, 1)
            V.tensor_scalar(cnt_i[:, 0:1], psW[0:NE, 1, 0:1], float(P - 1), None, ALU.add).then_inc(s_post, 1)
            dve.wait_ge(s_post, 1)
            V.tensor_scalar(cnt_i[:, 1:2], cnt_i[:, 0:1], 7, None, ALU.arith_shift_right).then_inc(s_post, 1)
            dve.wait_ge(s_post, 2)
            V.tensor_copy(nb_bf[:, :], cnt_i[:, 1:2]).then_inc(s_post, 1)
            dve.wait_ge(s_post, 3)
            V.tensor_copy(nb_row[:, :], bc(nb_bf[:, :], [NE, P])).then_inc(s_post, 1)
            dve.wait_ge(s_txn, NT)
            dve.wait_ge(s_xn_st, 16 * NT)
            dve.wait_ge(s_x1_st, 16 * NT)
            dve.wait_ge(s_post_pe, 1)
            V.tensor_copy(jend_col[:, :], psW[0:NE, 0, 2 * NE:2 * NE + 1]).then_inc(s_post, 1)
            dve.wait_ge(s_post, 5)
            V.tensor_scalar(ended[:, :], iota_j[:, :], jend_col[:, 0:1], None, ALU.is_ge).then_inc(s_post, 1)
            V.tensor_copy(base, psW[:, 0, 0:2 * NE]).then_inc(s_post, 1)
            V.memset(ring_i[:, 0:1], 0).then_inc(s_post, 1)
            dve.wait_ge(s_post, 8)
            V.tensor_copy(jend_i[:, :], base[:, NE:2 * NE]).then_inc(s_post_pe, 1)
            dve.wait_ge(s_post_pe, 3)
            V.tensor_scalar(ring_i[:, 1:JT + 1], psW[:, 1, 0:JT], 1.0, float(NE), ALU.add, ALU.min) \
             .then_inc(s_post_pe, 1)
            V.tensor_scalar(n_jobs[:, 0:1], base[:, 2 * NE - 1:2 * NE], 0.0, None, ALU.add).then_inc(s_post_pe, 1)
            dve.wait_ge(s_post_pe, 5)
            V.tensor_scalar(n_jobs[:, 1:2], n_jobs[:, 0:1], -2.0, None, ALU.add).then_inc(s_post, 1)
            dve.wait_ge(s_post, 9)
            V.tensor_scalar(n_jobs[:, 2:4], n_jobs[:, 0:2], 1, None, ALU.arith_shift_right).then_inc(s_n_jobs, 1)
            V.tensor_scalar(n_jobs[:, 4:6], n_jobs[:, 0:2], 2, None, ALU.arith_shift_right).then_inc(s_n_jobs, 1)
            dve.wait_ge(s_n_jobs, 2)
            V.scalar_tensor_tensor(out=n_jobs[:, 6:8], in0=n_jobs[:, 4:6], scalar=-2.0, in1=n_jobs[:, 2:4],
                                   op0=ALU.mult, op1=ALU.add).then_inc(s_n_jobs, 1)
            V.scalar_tensor_tensor(out=n_jobs[:, 8:10], in0=n_jobs[:, 2:4], scalar=-2.0, in1=n_jobs[:, 0:2],
                                   op0=ALU.mult, op1=ALU.add).then_inc(s_n_jobs, 1)
            V.tensor_copy(posi, pos[:, :, :].rearrange("p t e -> p (t e)")).then_inc(s_post, 1)
            dve.wait_ge(s_post, 10)
            V.tensor_scalar(posi, posi, 7, None, ALU.arith_shift_right).then_inc(s_post, 1)
            dve.wait_ge(s_post, 11)
            V.tensor_copy(chunk, posi).then_inc(s_post, 1)
            dve.wait_ge(s_post, 12)
            V.scalar_tensor_tensor(out=within, in0=chunk, scalar=-float(P),
                                   in1=pos[:, :, :].rearrange("p t e -> p (t e)"), op0=ALU.mult, op1=ALU.add) \
             .then_inc(s_post, 1)
            dve.wait_ge(s_post, 13)
            V.scalar_tensor_tensor(out=within, in0=within, scalar=float(JT), in1=chunk, op0=ALU.mult, op1=ALU.add) \
             .then_inc(s_post, 1)
            dve.wait_ge(s_post, 14)
            V.tensor_tensor(addr, within.rearrange("p (t e) -> p t e", t=NT),
                            bc(base[:, 0:NE].unsqueeze(1), [P, NT, NE]), ALU.add).then_inc(s_post, 1)
            dve.wait_ge(s_post, 15)
            V.scalar_tensor_tensor(out=addr, in0=addr, scalar=1.0, in1=m_all[:, :, :], op0=ALU.add, op1=ALU.mult) \
             .then_inc(s_post, 1)
            dve.wait_ge(s_post, 16)

            def slots(t):
                b = 6 * t
                V.max(tops[:, t, :], addr[:, t, :]).then_inc(s_post_idx, 1)
                dve.wait_ge(s_post_idx, b + 1)
                V.tensor_scalar(slot_i[:, t * 8:(t + 1) * 8], tops[:, t, :], -1.0, None, ALU.add) \
                 .then_inc(s_post_idx, 1)
                V.tensor_tensor(eq, bc(addr[:, t, :].unsqueeze(1), [P, 8, NE]), bc(tops[:, t, :].unsqueeze(2), [P, 8, NE]),
                                ALU.is_equal).then_inc(s_post_idx, 1)
                dve.wait_ge(s_post_idx, b + 3)
                V.tensor_tensor(eq, eq, bc(w_all[:, t, :].unsqueeze(1), [P, 8, NE]), ALU.mult).then_inc(s_post_idx, 1)
                dve.wait_ge(s_post_idx, b + 4)
                V.tensor_reduce(nbf[:, 0:8], eq, AX.X, ALU.add).then_inc(s_post_idx, 1)
                dve.wait_ge(s_post_idx, b + 5)
                V.tensor_copy(pay[:, t, :, 1], nbf[:, 0:8]).then_inc(s_post_idx, 1)

            def add_shared(j, par):
                dve.wait_ge(s_down, j + 1)
                dve.wait_ge(sh_x1[par], 16 * (j // 2 + 1))
                if j >= 2:
                    dve.wait_ge(sh_st[par], 16 * (j // 2))
                V.tensor_tensor(ysb[:, par], psW[:, 2:4, :].rearrange("p a n -> p (a n)"), x1l[:, par], ALU.add) \
                 .then_inc(s_y_ready, 1)

            slots(0)
            read_xT(1)
            h_mul(0, 0, one_col[:, 0:1])
            for j in range(NSH):
                if j >= 1:
                    h_mul(j, j % 2, one_col[:, 0:1])
                    read_xT(j + 1)
                    add_shared(j - 1, (j - 1) % 2)
                for t in range(2 * j + 1, min(2 * j + 3, NT)):
                    slots(t)
            dve.wait_ge(s_added, 16)
            h_mul(NSH, 0, tab[:, 0, 1:2])
            add_shared(NSH - 1, (NSH - 1) % 2)
            read_xT(NSH + 1)
            h_mul(NSH + 1, 1, tab[:, 1, 1:2])
            read_xT(NSH + 2)

            def jobs(i, ks):
                for k in ks:
                    j = i * 2 + (NSH + 2 + k)
                    h_mul(j, k, tab[:, bass.ds(i * 2 + (2 + k), 1), 1:2].rearrange("p a b -> p (a b)"))
                    read_xT(j + 1)

            routed_jobs(dve, 1, jobs)


_INS = ["x", "mix_norm_w", "w_in", "conv_w", "q_norm_w", "k_norm_w", "sinks", "conv_out_norm_w", "attn_out_norm_w",
        "w_out", "ffn_norm_w", "w_router", "router_bias", "w_exp_gate", "w_exp_up", "w_exp_down", "w_sh_gate",
        "w_sh_up", "w_sh_down"]


def kernel(**inputs):
    import numpy as _np
    import concourse.bacc as _bacc
    from concourse import mybir as _mybir
    from concourse.bass_utils import run_bass_kernel_spmd as _run

    nc = _bacc.Bacc("TRN2", target_bir_lowering=False, num_devices=1)
    arrays, args = {}, []
    for name in _INS:
        a = _np.ascontiguousarray(inputs[name])
        arrays[f"in_{name}_dram"] = a
        args.append(nc.dram_tensor(f"in_{name}_dram", a.shape, _mybir.dt.from_np(a.dtype), kind="ExternalInput").ap())
    shape = inputs["x"].shape
    args.append(nc.dram_tensor("out_0_dram", shape, _mybir.dt.from_np(_np.dtype("float32")),
                               kind="ExternalOutput").ap())
    hymba_moe(nc, *args)
    r = _run(nc, [arrays], core_ids=[0])
    return r.results[0]["out_0_dram"]
```
